# Optimizing a Trainium2 kernel written in Bass

```python
import jax, jax.numpy as jnp
from jax import lax
import numpy as np

D_MODEL = 1024
BATCH = 1
SEQ = 512
DEPTH = 2

CHUNK = 64
N_MIXERS = 2
FOX_HEADS = 16
FOX_HEAD_DIM = D_MODEL // FOX_HEADS
FOX_Q_BLOCK = 128
FOX_IN = 3 * D_MODEL + FOX_HEADS
GLA_HEADS = 4
GLA_KEY_DIM = D_MODEL // 2
GLA_VAL_DIM = D_MODEL
GLA_DK = GLA_KEY_DIM // GLA_HEADS
GLA_DV = GLA_VAL_DIM // GLA_HEADS
GLA_GATE_RANK = 16
GLA_GATE_TAU = 16.0
GLA_IN = 2 * GLA_KEY_DIM + GLA_VAL_DIM + GLA_GATE_RANK + GLA_VAL_DIM
D_FF = 4 * D_MODEL
EPS = 1e-6
N_FOX_LAYERS = (DEPTH + 1) // 2
N_GLA_LAYERS = DEPTH // 2

kernel_name = 'fox_gla_hybrid_trunk'

def rms_norm(x, g):
    xf = x.astype(jnp.float32)
    y = xf * lax.rsqrt(jnp.mean(xf * xf, axis=-1, keepdims=True) + EPS)
    return (y * g.astype(jnp.float32)).astype(x.dtype)

def fox_mixer(h, w_in, b_f, w_out):
    B, S, _ = h.shape
    H, HD, QB = FOX_HEADS, FOX_HEAD_DIM, FOX_Q_BLOCK
    proj = h @ w_in
    q, k, v, f_logit = jnp.split(proj, [D_MODEL, 2 * D_MODEL, 3 * D_MODEL], axis=-1)
    q = q.reshape(B, S, H, HD)
    k = k.reshape(B, S, H, HD)
    v = v.reshape(B, S, H, HD)
    log_f = jax.nn.log_sigmoid((f_logit + b_f).astype(jnp.float32))
    c = jnp.cumsum(log_f, axis=1).transpose(0, 2, 1)
    nqb = S // QB
    q_blocks = q.reshape(B, nqb, QB, H, HD).transpose(1, 0, 3, 2, 4)
    cq_blocks = c.reshape(B, H, nqb, QB).transpose(2, 0, 1, 3)
    t_blocks = jnp.arange(S).reshape(nqb, QB)
    k_pos = jnp.arange(S)
    scale = HD ** -0.5

    def block(args):
        qb, cqb, tb = args
        logits = jnp.einsum('bhqd,bshd->bhqs', qb, k).astype(jnp.float32) * scale
        logits = logits + cqb[..., :, None] - c[:, :, None, :]
        mask = k_pos[None, :] <= tb[:, None]
        logits = jnp.where(mask, logits, -jnp.inf)
        p = jax.nn.softmax(logits, axis=-1)
        return jnp.einsum('bhqs,bshd->bqhd', p.astype(v.dtype), v)

    o = lax.map(block, (q_blocks, cq_blocks, t_blocks))
    o = o.transpose(1, 0, 2, 3, 4).reshape(B, S, D_MODEL)
    return o @ w_out

def gla_mixer(h, w_in, w_gate_up, b_gate, g_norm, w_out):
    B, S, _ = h.shape
    H, DK, DV, C = GLA_HEADS, GLA_DK, GLA_DV, CHUNK
    n = S // C
    proj = h @ w_in
    splits = [GLA_KEY_DIM, 2 * GLA_KEY_DIM, 2 * GLA_KEY_DIM + GLA_VAL_DIM,
              2 * GLA_KEY_DIM + GLA_VAL_DIM + GLA_GATE_RANK]
    q, k, v, z_lr, r = jnp.split(proj, splits, axis=-1)
    g = jax.nn.log_sigmoid((z_lr @ w_gate_up + b_gate).astype(jnp.float32)) / GLA_GATE_TAU

    def to_chunks(t, d):
        return t.astype(jnp.float32).reshape(B, n, C, H, d).transpose(1, 0, 3, 2, 4)

    qc = to_chunks(q, DK) * (DK ** -0.5)
    kc = to_chunks(k, DK)
    vc = to_chunks(v, DV)
    bc = jnp.cumsum(to_chunks(g, DK), axis=3)
    causal = jnp.tril(jnp.ones((C, C), dtype=bool))

    def step(state, inp):
        qj, kj, vj, bj = inp
        diff = bj[:, :, :, None, :] - bj[:, :, None, :, :]
        decay = jnp.exp(jnp.where(causal[:, :, None], diff, -jnp.inf))
        attn = jnp.einsum('bhtk,bhsk,bhtsk->bhts', qj, kj, decay)
        o = jnp.einsum('bhts,bhsv->bhtv', attn, vj) + \
            jnp.einsum('bhtk,bhkv->bhtv', qj * jnp.exp(bj), state)
        b_last = bj[:, :, -1, :]
        k_dec = kj * jnp.exp(b_last[:, :, None, :] - bj)
        state = state * jnp.exp(b_last)[..., None] + jnp.einsum('bhsk,bhsv->bhkv', k_dec, vj)
        return state, o

    state0 = jnp.zeros((B, H, DK, DV), jnp.float32)
    _, o = lax.scan(step, state0, (qc, kc, vc, bc))
    o = o.transpose(1, 0, 3, 2, 4).reshape(B, S, H, DV)
    o = o * lax.rsqrt(jnp.mean(o * o, axis=-1, keepdims=True) + EPS) * g_norm.astype(jnp.float32)
    o = o * jax.nn.silu(r.astype(jnp.float32)).reshape(B, S, H, DV)
    return o.reshape(B, S, D_MODEL).astype(h.dtype) @ w_out

def sqrelu_mlp(h, w_up, w_down):
    return jnp.square(jax.nn.relu(h @ w_up)) @ w_down

def setup_inputs(seed: int = 0) -> dict:
    key = jax.random.key(seed)
    ks = jax.random.split(key, 14)
    D = D_MODEL
    nrm = jax.random.normal
    x = nrm(ks[0], (BATCH, SEQ, D), jnp.float32)
    fox_w_in = nrm(ks[1], (N_FOX_LAYERS, D, FOX_IN), jnp.float32) * D ** -0.5
    fox_b_f = jax.random.uniform(ks[2], (N_FOX_LAYERS, FOX_HEADS), jnp.float32, 0.0, 3.0)
    fox_w_out = nrm(ks[3], (N_FOX_LAYERS, D, D), jnp.float32) * D ** -0.5
    gla_w_in = nrm(ks[4], (N_GLA_LAYERS, D, GLA_IN), jnp.float32) * D ** -0.5
    gla_w_gate_up = nrm(ks[5], (N_GLA_LAYERS, GLA_GATE_RANK, GLA_KEY_DIM), jnp.float32) * GLA_GATE_RANK ** -0.5
    gla_b_gate = 0.1 * nrm(ks[6], (N_GLA_LAYERS, GLA_KEY_DIM), jnp.float32)
    gla_norm_g = 1.0 + 0.05 * nrm(ks[7], (N_GLA_LAYERS, GLA_DV), jnp.float32)
    gla_w_out = nrm(ks[8], (N_GLA_LAYERS, GLA_VAL_DIM, D), jnp.float32) * GLA_VAL_DIM ** -0.5
    mlp_w_up = nrm(ks[9], (DEPTH, D, D_FF), jnp.float32) * D ** -0.5
    mlp_w_down = nrm(ks[10], (DEPTH, D_FF, D), jnp.float32) * D_FF ** -0.5
    norm_mix_g = 1.0 + 0.05 * nrm(ks[11], (DEPTH, D), jnp.float32)
    norm_mlp_g = 1.0 + 0.05 * nrm(ks[12], (DEPTH, D), jnp.float32)
    norm_final_g = 1.0 + 0.05 * nrm(ks[13], (D,), jnp.float32)
    return {'x': x, 'fox_w_in': fox_w_in, 'fox_b_f': fox_b_f, 'fox_w_out': fox_w_out,
            'gla_w_in': gla_w_in, 'gla_w_gate_up': gla_w_gate_up, 'gla_b_gate': gla_b_gate,
            'gla_norm_g': gla_norm_g, 'gla_w_out': gla_w_out,
            'mlp_w_up': mlp_w_up, 'mlp_w_down': mlp_w_down,
            'norm_mix_g': norm_mix_g, 'norm_mlp_g': norm_mlp_g, 'norm_final_g': norm_final_g}

def reference(x, fox_w_in, fox_b_f, fox_w_out, gla_w_in, gla_w_gate_up, gla_b_gate,
              gla_norm_g, gla_w_out, mlp_w_up, mlp_w_down, norm_mix_g, norm_mlp_g,
              norm_final_g):
    h = x
    for i in range(DEPTH):
        j = i // N_MIXERS
        hn = rms_norm(h, norm_mix_g[i])
        if i % N_MIXERS == 0:
            h = h + fox_mixer(hn, fox_w_in[j], fox_b_f[j], fox_w_out[j])
        else:
            h = h + gla_mixer(hn, gla_w_in[j], gla_w_gate_up[j], gla_b_gate[j],
                              gla_norm_g[j], gla_w_out[j])
        h = h + sqrelu_mlp(rms_norm(h, norm_mlp_g[i]), mlp_w_up[i], mlp_w_down[i])
    return rms_norm(h, norm_final_g)


_drawn_inputs = setup_inputs


def setup_inputs(seed=0):
    import zlib

    import numpy as np

    out = dict(_drawn_inputs(seed))
    spreads = {}
    factors = {'gla_b_gate': 2.983, 'gla_norm_g': 3.142}
    for name, (base, spread) in spreads.items():
        noise = np.random.default_rng([zlib.crc32(name.encode()), seed]).standard_normal(out[name].shape)
        drawn = base * np.exp(spread * noise) if base else spread * noise
        out[name] = __import__('jax').numpy.asarray(drawn.astype(out[name].dtype))
    for name, factor in factors.items():
        out[name] = (out[name] * factor).astype(out[name].dtype)
    return out
```

```python
from contextlib import ExitStack

import concourse.bass as bass
from concourse import mybir

F32 = mybir.dt.float32
F32R = mybir.dt.float32r
BF16 = mybir.dt.bfloat16
I32 = mybir.dt.int32
U8 = mybir.dt.uint8
ALU = mybir.AluOpType
ACT = mybir.ActivationFunctionType
AX_X = mybir.AxisListType.X
ds = bass.ds

P = 128
S = 512
TB = S // P
D = 1024
KT = D // P
EPS = 1e-6
DFF = 4 * D
FOX_H = 16
FOX_HD = D // FOX_H
PAIRS = FOX_H // 2
GLA_H = 4
GLA_K = D // 2
DK = GLA_K // GLA_H
DV = D // GLA_H
RANK = 16
TAU = 16.0
ROOT_D = 32.0
ROOT_DV = 16.0
assert ROOT_D ** 2 == D and ROOT_DV ** 2 == DV
LEVELS = 7
MASKED = -1e30
TRI = P * TB * (TB + 1) // 2
OFF = [P * t * (t + 1) // 2 for t in range(TB)]
SCORES = ((3, 2, 0), (2, 3, 0), (1, 4, 0), (0, 4, 2 * P))
TURNED = ((5, tuple((t, 0, t * P) for t in range(4))),
          (6, tuple((t, 1, (t - 1) * P) for t in range(1, 4)) + ((3, 3, 3 * P),)),
          (7, tuple((t, 2, (t - 2) * P) for t in range(2, 4))))
LEVEL_BANK = (7, 0)
GAIN = (0, 2, 1, 3)
GO_BASE = 1

SLOTS = 4
UNIT = 2048
FOX_U = 0
FOX_OUT_U = FOX_U + 2 * PAIRS
MLP0_U = FOX_OUT_U + 4
GROUPS = DFF // D
GLA_U = MLP0_U + 8 * GROUPS
GLA_OUT_U = GLA_U + 4 * GLA_H
MLP1_U = GLA_OUT_U + 4
UNITS = MLP1_U + 8 * GROUPS
FOX_ADDS = 0
MLP0_ADDS = FOX_ADDS + 8
GLA_ADDS = MLP0_ADDS + 8 * GROUPS
MLP1_ADDS = GLA_ADDS + 8
ADDS = MLP1_ADDS + 8 * GROUPS


class Steps:

    def __init__(self, eng, sem):
        self.eng, self.sem, self.n, self.turns = eng, sem, 0, 0

    def enter(self, turn, per):
        self.turns, self.per, self.at = turn * per, per, self.n

    def leave(self, turns):
        assert self.n - self.at == self.per
        self.n, self.turns = self.at + turns * self.per, 0

    def then(self, ins):
        ins.then_inc(self.sem, 1)
        self.n += 1
        self.eng.wait_ge(self.sem, self.turns + self.n)


def fox_gla_trunk(nc, x, fox_w_in, fox_b_f, fox_w_out, gla_w_in, gla_w_gate_up, gla_b_gate,
                  gla_norm_g, gla_w_out, mlp_w_up, mlp_w_down, norm_mix_g, norm_mlp_g,
                  norm_final_g, out):
    x_d = x.rearrange("a (t p) d -> (a t) p d", p=P)
    out_d = out.rearrange("a (t p) d -> (a t) p d", p=P)
    fox_in_d = fox_w_in.rearrange("a (k p) n -> (a p) k n", p=P)
    fox_out_d = fox_w_out.rearrange("a (k p) n -> (a p) k n", p=P)
    gla_in_d = gla_w_in.rearrange("a (k p) n -> (a p) k n", p=P)
    gla_out_d = gla_w_out.rearrange("a (k p) n -> (a p) k n", p=P)
    up_d = mlp_w_up.rearrange("a (k p) n -> a p k n", p=P)
    down_d = mlp_w_down.rearrange("a (k p) n -> a p k n", p=P)

    with ExitStack() as ctx:
        def sb(name, shape, dt=F32, at=ctx):
            return at.enter_context(nc.sbuf_tensor(name, shape, dt))

        def sem(name):
            return ctx.enter_context(nc.semaphore(name))

        w_stage = sb("w_stage", [P, SLOTS, UNIT])
        w_hi = sb("w_hi", [P, SLOTS, UNIT], F32R)
        w_lo = sb("w_lo", [P, SLOTS, UNIT], F32R)
        hT_hi = sb("hT_hi", [P, KT, S], F32R)
        hT_lo = sb("hT_lo", [P, KT, S], F32R)
        h = sb("h", [P, TB, D])
        ident = sb("ident", [P, P])
        gain = sb("gain", [P, 4, KT])
        ss = sb("ss", [P, 2, TB])
        rstd = sb("rstd", [P, TB])
        minus_half = sb("minus_half", [P, TB])
        eps = {c: sb(f"eps{c}", [P, TB]) for c in (D, DV)}
        gate_w = sb("gate_w", [P, 2, KT, RANK])
        gate_hi = sb("gate_hi", [P, 2, KT, RANK], F32R)
        gate_lo = sb("gate_lo", [P, 2, KT, RANK], F32R)

        with ExitStack() as mem:
            hn = sb("hn", [P, TB, D], at=mem)

        with ExitStack() as mem:
            qz = sb("qz", [P, 2, 2, S], at=mem)
            kT = sb("kT", [P, S], at=mem)
            vT = sb("vT", [P, S], at=mem)
            v = sb("v", [P, TB, P], at=mem)
            with ExitStack() as gates:
                fg = sb("fg", [FOX_H, 2, S], at=gates)
                fg16 = sb("fg16", [FOX_H, 2, S], BF16, gates)
                gain_rows = sb("gain_rows", [4 * KT, P], at=gates)
            probs = sb("probs", [P, TRI], at=mem)
            probsT = sb("probsT", [P, TRI], at=mem)
            ident16 = sb("ident16", [P, P], BF16, mem)
            causal16 = sb("causal16", [P, P], BF16, mem)
            sel = sb("sel", [96, FOX_H], BF16, mem)
            c3 = sb("c3", [96, S], BF16, mem)
            mx = sb("mx", [P, TB], at=mem)
            nmx = sb("nmx", [P, 2, TB], at=mem)
            rsum = sb("rsum", [P, TB], at=mem)
            rinv = sb("rinv", [P, TB], at=mem)
            bf_col = sb("bf_col", [FOX_H, 1], at=mem)
            oT_hi = sb("oT_hi", [P, KT, S], F32R, mem)
            oT_lo = sb("oT_lo", [P, KT, S], F32R, mem)

        with ExitStack() as mem:
            relu = sb("relu", [P, 4, S], at=mem)
            u_sq = sb("u_sq", [P, 4, S], at=mem)
            u_hi = sb("u_hi", [P, KT, S], F32R, mem)
            u_lo = sb("u_lo", [P, KT, S], F32R, mem)
            fgain = sb("fgain", [P, D], at=mem)

        with ExitStack() as mem:
            o_all = sb("o_all", [P, TB, D], at=mem)
            gq = sb("gq", [P, S], at=mem)
            gk = sb("gk", [P, S], at=mem)
            gv = sb("gv", [P, TB, DV], at=mem)
            silu = sb("silu", [P, TB, DV], at=mem)
            gb = sb("gb", [P, GLA_H, S], at=mem)
            with ExitStack() as gates:
                zT = sb("zT", [32, S], at=gates)
                glog = sb("glog", [P, GLA_H, S], at=gates)
                gup = sb("gup", [RANK + 1, GLA_K], at=gates)
                xor = sb("xor", [P, P], I32, gates)
                other = sb("other", [P, P], I32, gates)
                ge = sb("ge", [P, P], at=gates)
                restart = sb("restart", [P, TB, P], BF16, gates)
            decay = sb("decay", [P, 2, S], at=mem)
            ql = sb("ql", [P, 2, S], at=mem)
            kl = sb("kl", [P, 2, S], at=mem)
            tail = sb("tail", [P, TB - 1, P], at=mem)
            since = sb("since", [P, TB, P], at=mem)
            through = sb("through", [P, TB], at=mem)
            tailT = sb("tailT", [P, TB - 1, P], at=mem)
            attnT = sb("attnT", [P, TB, P], at=mem)
            state = sb("state", [P, TB - 1, DV], at=mem)
            gn = sb("gn", [P, DV], at=mem)
            masks = sb("masks", [P, LEVELS, P], U8, mem)
            turn = sb("turn", [1, 1], at=mem)
            oss = sb("oss", [P, TB], at=mem)
            orstd = sb("orstd", [P, TB], at=mem)

        bank = [ctx.enter_context(nc.psum_tensor(f"bank{i}", [P, S], F32)) for i in range(8)]

        x_loaded = [sem(f"x_loaded{t}") for t in range(TB)]
        gain_loaded, gain_turned, gain_made = sem("gain_loaded"), sem("gain_turned"), sem("gain_made")
        gate_w_loaded, bf_loaded = sem("gate_w_loaded"), sem("bf_loaded")
        gup_loaded, gn_loaded, fgain_loaded = sem("gup_loaded"), sem("gn_loaded"), sem("fgain_loaded")
        out_stored, fgain_scaled, gn_scaled = sem("out_stored"), sem("fgain_scaled"), sem("gn_scaled")
        w_loaded = [sem(f"w_loaded{s}") for s in range(SLOTS)]
        k_loaded = [sem(f"k_loaded{s}") for s in range(2)]
        w_hi_made, w_lo_made, w_begun = sem("w_hi_made"), sem("w_lo_made"), sem("w_begun")
        gate_hi_made, gate_lo_made = sem("gate_hi_made"), sem("gate_lo_made")
        pool_step, ident_made, fox_consts_made, qz_zeroed = (
            sem("pool_step"), sem("ident_made"), sem("fox_consts_made"), sem("qz_zeroed"))
        gla_filled, xor_made, xor_cut, masks_made = (
            sem("gla_filled"), sem("xor_made"), sem("xor_cut"), sem("masks_made"))
        levels_zeroed = sem("levels_zeroed")
        dve_step, act_step = sem("dve_step"), sem("act_step")
        squared, hn_made, hn_turned, hT_hi_made, hT_lo_made = (
            sem("squared"), sem("hn_made"), sem("hn_turned"), sem("hT_hi_made"), sem("hT_lo_made"))
        rstd_made, y_made = sem("rstd_made"), sem("y_made")
        added, sum_done = sem("added"), sem("sum_done")
        up_done, relu_made, u_made, u_hi_made, u_lo_made = (
            sem("up_done"), sem("relu_made"), sem("u_made"), sem("u_hi_made"), sem("u_lo_made"))
        f_done, f_abs, f_ln, c3_made = sem("f_done"), sem("f_abs"), sem("f_ln"), sem("c3_made")
        q_done, k_done, vT_done, v_turned = sem("q_done"), sem("k_done"), sem("vT_done"), sem("v_turned")
        q_copied, k_copied, vT_copied, v_copied = (
            sem("q_copied"), sem("k_copied"), sem("vT_copied"), sem("v_copied"))
        scores_done, nmx_made, exp_made, probs_made = (
            sem("scores_done"), sem("nmx_made"), sem("exp_made"), sem("probs_made"))
        probs_turned, pT_act, pT_dve = sem("probs_turned"), sem("pT_act"), sem("pT_dve")
        o_done, o_hi_made, o_lo_made = sem("o_done"), sem("o_hi_made"), sem("o_lo_made")
        z_done, z_copied = sem("z_done"), sem("z_copied")
        gq_done, gk_done, gq_copied, gk_copied = (
            sem("gq_done"), sem("gk_done"), sem("gq_copied"), sem("gk_copied"))
        gate_done, g_abs, g_min, g_ln, gb_made = (
            sem("gate_done"), sem("g_abs"), sem("g_min"), sem("g_ln"), sem("gb_made"))
        gv_done, gv_copied, r_done, er_made, silu_made = (
            sem("gv_done"), sem("gv_copied"), sem("r_done"), sem("er_made"), sem("silu_made"))
        half_diff, diff_made, decay_made, ql_made, level_done, level_kept, orstd_made = (
            sem("half_diff"), sem("diff_made"), sem("decay_made"), sem("ql_made"), sem("level_done"),
            sem("level_kept"), sem("orstd_made"))
        since_exp, qsince_made, tail_diff, tail_exp, ktail_made, tail_turned, tailT_made = (
            sem("since_exp"), sem("qsince_made"), sem("tail_diff"), sem("tail_exp"), sem("ktail_made"),
            sem("tail_turned"), sem("tailT_made"))
        kv_done, state_made, through_made = sem("kv_done"), sem("state_made"), sem("through_made")
        go_done, go_squared, go_made = sem("go_done"), sem("go_squared"), sem("go_made")
        go_turned, goT_hi_made, goT_lo_made = sem("go_turned"), sem("goT_hi_made"), sem("goT_lo_made")

        block = ctx.enter_context(nc.Block())

        def fp(ap):
            return ap.bitcast(F32)

        def flat(ap):
            return ap.rearrange("p c n -> p (c n)")

        def halves(ap, half):
            two = ap.rearrange("p (n two s) -> p n two s", two=2, s=half)
            return two[:, :, 0, :], two[:, :, 1, :]

        def cols(buf, slot, c, first=0):
            return buf[:, slot, first:first + KT * c].rearrange("p (k n) -> p k n", k=KT)

        def sum_bank(half, t, early):
            return 4 * (half if early and t == 0 else 1 - half) + t

        @block.sync
        def _(sp):
            def load(i, per, c, dst, src):
                if not (isinstance(i, int) and i * per + c < SLOTS):
                    sp.wait_ge(w_lo_made, i * per + (c - SLOTS + 1))
                sp.dma_start(dst, src).then_inc(w_loaded[c % SLOTS], 16)

            def load_fox(i, n, c):
                pair = n * 2 + i
                load(n, 4, c, cols(w_stage, c % 4, P), fox_in_d[:, :, ds(pair * P, P)])
                sp.dma_start(cols(w_stage, c % 4, P, UNIT // 2),
                             fox_in_d[:, :, ds(pair * P + D, P)]).then_inc(k_loaded[c % 4 // 2], 16)
                load(n, 4, c + 1, cols(w_stage, (c + 1) % 4, P), fox_in_d[:, :, ds(pair * P + 2 * D, P)])

            def load_rows(i, per, c, src, row):
                for j in range(4):
                    if c + j == FOX_OUT_U:
                        dst = w_stage[:, 0, :].rearrange("p (k n) -> p k n", k=KT // 2)
                        load(i, per, c, dst[:, 0:2, :], src[:, 0:2, 0:S])
                        sp.dma_start(dst[:, 2:4, :], src[:, 2:4, 0:S]).then_inc(k_loaded[0], 16)
                        continue
                    load(i, per, c + j, w_stage[:, j, :].rearrange("p (k n) -> p k n", k=KT // 2),
                         src[:, ds(row + (j % 2) * (KT // 2), KT // 2), (j // 2) * S:(j // 2 + 1) * S])

            def load_mlp(layer, c):
                with sp.Fori(0, GROUPS) as g:
                    for j in range(4):
                        load(g, 8, c + j, cols(w_stage, j, 256), up_d[layer][:, :, ds(g * D + j * 256, 256)])
                    load_rows(g, 8, c + 4, down_d[layer], g * KT)

            for t in range(0, TB, 2):
                sp.dma_start(h[:, t, :], x_d[t]).then_inc(x_loaded[t], 16)
            for i in range(2):
                load_fox(i, 0, FOX_U + 2 * i)
            with sp.Fori(1, PAIRS // 2) as n:
                for i in range(2):
                    load_fox(i, n, FOX_U + 2 * i)
            load_rows(0, 0, FOX_OUT_U, fox_out_d, 0)
            load_mlp(0, MLP0_U)
            with sp.Fori(0, GLA_H) as a:
                for j, (first, c) in enumerate(((0, DK), (GLA_K, DK), (2 * GLA_K, DV), (2 * GLA_K + D + RANK, DV))):
                    load(a, 4, GLA_U + j, cols(w_stage, j, c), gla_in_d[:, :, ds(a * c + first, c)])
            load_rows(0, 0, GLA_OUT_U, gla_out_d, 0)
            load_mlp(1, MLP1_U)
            for t in range(TB):
                sp.wait_ge(y_made, t + 1)
                sp.dma_start(out_d[t], hn[:, t, :]).then_inc(out_stored, 16)
            sp.wait_ge(out_stored, 16 * TB)

        @block.gpsimd
        def _(pool):
            mine = Steps(pool, pool_step)
            step = mine.then

            def select(ap, op, value, base, pattern, mult=1):
                return pool.affine_select(out=ap, in_=ap, compare_op=op, fill=value, base=base,
                                          pattern=pattern, channel_multiplier=mult)

            def rsqrt(to, squares, more, columns):
                to = to[:, columns]
                step(pool.tensor_tensor(to, squares[:, columns], more[:, columns], ALU.add))
                return pool.tensor_tensor(to, to, minus_half[:, columns], ALU.pow)

            def norm(n):
                if n:
                    pool.wait_ge(squared, n * 2 * TB)
                    step(pool.tensor_tensor(ss[:, 0, :], ss[:, 0, :], eps[D][:], ALU.add))
                for t in range(TB):
                    pool.wait_ge(squared, n * 2 * TB + t + 1)
                    rsqrt(rstd, ss[:, 1, :], ss[:, 0, :] if n else eps[D], slice(t, t + 1)).then_inc(rstd_made, 1)

            step(pool.memset(ident[:], 0.0))
            step(pool.memset(minus_half[:], -0.5))
            for count in eps:
                step(pool.memset(eps[count][:], EPS * count))
            select(ident[:], ALU.not_equal, 1.0, 0, [[-1, P]]).then_inc(ident_made, 1)
            norm(0)
            step(pool.memset(ident16[:], 0.0))
            select(ident16[:], ALU.not_equal, 1.0, 0, [[-1, P]]).then_inc(fox_consts_made, 1)
            step(pool.memset(causal16[:], 0.0))
            select(causal16[:], ALU.is_ge, MASKED, 0, [[-1, P]]).then_inc(fox_consts_made, 1)
            step(pool.memset(sel[:], 0.0))
            for j in range(3):
                step(select(sel[:], ALU.not_equal, -1.0, -32 * j, [[-1, FOX_H]]))
            pool.memset(c3[:], 0.0).then_inc(fox_consts_made, 1)
            pool.wait_ge(hn_turned, KT)
            pool.wait_ge(fox_consts_made, 3)
            pool.memset(qz[FOX_HD:P, :, 0, :], 0.0).then_inc(qz_zeroed, 1)
            pool.wait_ge(qz_zeroed, 1)
            pool.memset(qz[0:FOX_HD, :, 1, :], 0.0).then_inc(qz_zeroed, 1)

            norm(1)
            norm(2)
            pool.wait_ge(hn_turned, 3 * KT)
            pool.memset(zT[:], 1.0).then_inc(gla_filled, 1)
            pool.iota(xor[:], pattern=[[0, P]], base=0, channel_multiplier=1).then_inc(gla_filled, 1)
            pool.iota(other[:], pattern=[[1, P]], base=0, channel_multiplier=0).then_inc(gla_filled, 1)
            pool.memset(restart[:], 1.0).then_inc(gla_filled, 1)
            pool.wait_ge(gla_filled, 4)
            pool.memset(restart[:, :, 0:1], 0.0).then_inc(gla_filled, 1)
            pool.wait_ge(xor_made, 1)
            select(xor[:], ALU.is_gt, 0.0, 0, [[1, P]], -1).then_inc(xor_cut, 1)
            pool.wait_ge(gb_made, GLA_H)
            pool.wait_ge(masks_made, LEVELS)
            pool.memset(ql[:], 0.0).then_inc(levels_zeroed, 1)
            pool.memset(kl[:], 0.0).then_inc(levels_zeroed, 1)
            with pool.Fori(0, GLA_H) as a:
                mine.enter(a, 2)
                pool.wait_ge(tail_exp, a + 1)
                pool.wait_ge(gk_copied, a + 1)
                pool.tensor_tensor(tail[:], tail[:], gk[:, 0:(TB - 1) * P].rearrange("p (c n) -> p c n", c=TB - 1),
                                   ALU.mult).then_inc(ktail_made, 1)
                pool.wait_ge(through_made, a + 1)
                pool.wait_ge(gq_copied, a + 1)
                pool.tensor_tensor(flat(since[:]), flat(since[:]), gq[:], ALU.mult).then_inc(qsince_made, 1)
                for j in range(2):
                    pool.wait_ge(go_squared, a * TB + (2 * j + 2))
                    rsqrt(orstd, oss, eps[DV], slice(2 * j, 2 * j + 2)).then_inc(orstd_made, 1)
            mine.leave(GLA_H)
            norm(3)
            norm(4)

        @block.scalar
        def _(act):
            mine = Steps(act, act_step)

            for t in range(1, TB, 2):
                act.dma_start(h[:, t, :], x_d[t]).then_inc(x_loaded[t], 16)
            for j, g in enumerate((norm_mix_g, norm_mlp_g)):
                act.dma_start(gain_rows[16 * j:16 * j + 16, :],
                              g.rearrange("l (k p) -> (l k) p", p=P)).then_inc(gain_loaded, 16)
            act.dma_start(bf_col[:], fox_b_f.rearrange("a h -> h a"), allow_slow_non_contiguous=True).then_inc(bf_loaded, 16)
            act.dma_start(gate_w[:, 0, :, :], fox_in_d[:, :, 3 * D:3 * D + FOX_H]).then_inc(gate_w_loaded, 16)
            act.dma_start(gate_w[:, 1, :, :],
                          gla_in_d[:, :, 2 * GLA_K + D:2 * GLA_K + D + RANK]).then_inc(gate_w_loaded, 16)

            def split_hi(i, per, c, n=UNIT, keys=False):
                slot = c % SLOTS
                act.wait_ge(w_loaded[slot], (i * (per // SLOTS) + (c // SLOTS + 1)) * 16)
                if keys:
                    act.wait_ge(k_loaded[slot // 2], (i * (per // SLOTS) + (c // SLOTS + 1)) * 16)
                if not (isinstance(i, int) and i * per + c < SLOTS):
                    act.wait_ge(w_begun, i * per + (c - SLOTS + 2))
                act.activation(w_hi[:, slot, 0:n], w_stage[:, slot, 0:n], ACT.Copy).then_inc(w_hi_made, 1)

            def norm(n, adds=0):
                for half in range(2) if n else ():
                    for t in range(TB):
                        act.wait_ge(added, adds - 2 * TB + TB * half + t + 1)
                        part = slice(half * S, (half + 1) * S)
                        act.activation(hn[:, t, part], h[:, t, part], ACT.Square,
                                       accum_out=ss[:, half, t:t + 1]).then_inc(squared, 1)
                if n == 4:
                    return
                for k in range(KT):
                    act.wait_ge(hn_turned, n * KT + k + 1)
                    act.activation(hT_hi[:, k, :], bank[k][:], ACT.Copy,
                                   scale=gain[:, GAIN[n], k:k + 1]).then_inc(hT_hi_made, 1)

            def out_slots(c):
                for j in range(4):
                    split_hi(0, 0, c + j + 3)

            def mlp(layer, c):
                tiles = layer * 8 * GROUPS

                def group(g, last=False):
                    for j in range(8):
                        if not (last and layer == 1 and j >= 5):
                            split_hi(g, 8, c + j + 3)
                        for t in (2 * j, 2 * j + 1) if j < 4 else ():
                            act.wait_ge(up_done, g * 8 + (tiles + t + 1))
                            act.activation(relu[:, t % 4, :], bank[t % 4][:], ACT.Relu).then_inc(relu_made, 1)
                            act.wait_ge(relu_made, g * 8 + (tiles + t + 1))
                            act.activation(u_hi[:, t, :], relu[:, t % 4, :], ACT.Square).then_inc(u_hi_made, 1)

                with act.Fori(0, GROUPS - 1) as g:
                    group(g)
                group(GROUPS - 1, True)

            for t in range(TB):
                act.wait_ge(x_loaded[t], 16)
                act.activation(hn[:, t, :], h[:, t, :], ACT.Square, accum_out=ss[:, 1, t:t + 1]).then_inc(squared, 1)
            act.wait_ge(gain_turned, 1)
            act.activation(gain[:].rearrange("p n k -> p (n k)"), bank[7][:, 0:4 * KT], ACT.Copy).then_inc(gain_made, 1)
            act.wait_ge(gain_made, 1)
            split_hi(0, 0, 0, UNIT, True)
            norm(0)
            act.wait_ge(gate_w_loaded, 32)
            act.activation(gate_hi[:], gate_w[:], ACT.Copy).then_inc(gate_hi_made, 1)
            split_hi(0, 0, 1, UNIT // 2)
            split_hi(0, 0, 2, UNIT, True)

            def copy_q(i, par):
                act.wait_ge(q_done, i + 1)
                for a in range(2):
                    rows = slice(a * FOX_HD, (a + 1) * FOX_HD)
                    act.activation(qz[rows, par, a, :], bank[0][rows, :], ACT.Copy,
                                   scale=FOX_HD ** -0.5).then_inc(q_copied, 1)

            def copy_k(i):
                act.wait_ge(k_done, i + 1)
                act.activation(kT[:], bank[0][:], ACT.Copy).then_inc(k_copied, 1)

            def exps(head, a):
                for m, (t, b, first) in enumerate(SCORES):
                    act.wait_ge(nmx_made, head * 3 + min(m, 2) + 1)
                    w = (t + 1) * P
                    act.activation(probs[:, OFF[t]:OFF[t] + w], bank[b][:, first:first + w], ACT.Exp,
                                   bias=nmx[:, a, t:t + 1], accum_out=rsum[:, t:t + 1]).then_inc(exp_made, 1)

            def copy_pT(head):
                act.wait_ge(probs_turned, head * 3 + 1)
                act.activation(probsT[:, 0:512], bank[5][:], ACT.Copy).then_inc(pT_act, 1)
                act.wait_ge(probs_turned, head * 3 + 3)
                act.activation(probsT[:, 1024:1280], bank[7][:, 0:256], ACT.Copy).then_inc(pT_act, 1)

            def copy_o(i, a):
                rows = slice(a * FOX_HD, (a + 1) * FOX_HD)
                act.wait_ge(o_done, i * 2 + (a + 1))
                act.activation(oT_hi[rows, ds(i, 1), :].rearrange("p a n -> p (a n)"), bank[1][rows, :],
                               ACT.Copy).then_inc(o_hi_made, 1)

            def fox_pair(n, b, following=True):
                i = n * 2 + b
                exps(i * 2, 0)
                if following:
                    split_hi(n, 4, 2 * b + 5, UNIT // 2 if not isinstance(n, int) else UNIT)
                    copy_q(i + 1, 1 - b)
                copy_pT(i * 2)
                exps(i * 2 + 1, 1)
                copy_o(i, 0)
                if following:
                    copy_k(i + 1)
                copy_pT(i * 2 + 1)
                if following:
                    split_hi(n, 4, 2 * b + 6, UNIT, not isinstance(n, int))
                copy_o(i, 1)

            split_hi(0, 0, 3, UNIT // 2)
            act.wait_ge(qz_zeroed, 2)
            copy_q(0, 0)
            act.wait_ge(f_done, 1)
            act.wait_ge(bf_loaded, 16)
            act.activation(fg[:, 0, :], bank[1][0:FOX_H, :], ACT.Abs, bias=bf_col[:, 0:1]).then_inc(f_abs, 1)
            act.wait_ge(f_abs, 1)
            mine.then(act.activation(fg[:, 0, :], fg[:, 0, :], ACT.Exp, scale=-1.0))
            act.activation(fg[:, 0, :], fg[:, 0, :], ACT.Ln, bias=1.0).then_inc(f_ln, 1)
            copy_k(0)
            split_hi(0, 0, 4, UNIT, True)
            with act.Fori(0, PAIRS // 2 - 1) as n:
                fox_pair(n, 0)
                fox_pair(n, 1)
            fox_pair(PAIRS // 2 - 1, 0)
            fox_pair(PAIRS // 2 - 1, 1, False)
            out_slots(FOX_OUT_U)
            norm(1, MLP0_ADDS)
            mlp(0, MLP0_U)
            norm(2, GLA_ADDS)

            act.dma_start(gn[:], gla_norm_g.rearrange("a n -> (a n)").partition_broadcast(P)).then_inc(gn_loaded, 16)
            act.dma_start(gup[0:RANK, :], gla_w_gate_up[0]).then_inc(gup_loaded, 16)
            act.dma_start(gup[RANK:RANK + 1, :], gla_b_gate).then_inc(gup_loaded, 16)
            act.wait_ge(gla_filled, 1)
            act.wait_ge(z_done, 1)
            act.activation(zT[0:RANK, :], bank[0][0:RANK, :], ACT.Copy).then_inc(z_copied, 1)
            for a in range(GLA_H):
                act.wait_ge(gate_done, a + 1)
                act.activation(glog[:, a, :], bank[3 + a][:], ACT.Abs).then_inc(g_abs, 1)
            act.wait_ge(g_abs, GLA_H)
            mine.then(act.activation(glog[:], glog[:], ACT.Exp, scale=-1.0))
            act.wait_ge(gn_loaded, 16)
            act.activation(gn[:], gn[:], ACT.Copy, scale=ROOT_DV).then_inc(gn_scaled, 1)
            act.activation(glog[:], glog[:], ACT.Ln, bias=1.0).then_inc(g_ln, 1)

            with act.Fori(0, GLA_H) as a:
                def split(j):
                    split_hi(a, 4, GLA_U + j)

                def decays(lv):
                    act.wait_ge(diff_made, a * LEVELS + lv)
                    act.activation(decay[:, lv % 2, :], decay[:, lv % 2, :], ACT.Exp,
                                   scale=1.0 / TAU).then_inc(decay_made, 1)

                def copy_v(j):
                    act.wait_ge(gv_done, a * 2 + (j + 1))
                    act.activation(flat(gv[:, 2 * j:2 * j + 2, :]), bank[3 + j][:], ACT.Copy).then_inc(gv_copied, 1)

                def exp_r(j):
                    act.wait_ge(r_done, a * 2 + (j + 1))
                    act.activation(flat(silu[:, 2 * j:2 * j + 2, :]), bank[5 + j][:], ACT.Exp,
                                   scale=-1.0).then_inc(er_made, 1)

                split(3)
                act.wait_ge(gq_done, a + 1)
                act.activation(gq[:], bank[0][:], ACT.Copy, scale=DK ** -0.5).then_inc(gq_copied, 1)
                act.wait_ge(gb_made, GLA_H)
                act.activation(flat(since[:]), flat(gb[:, ds(a, 1), :]), ACT.Exp, scale=1.0 / TAU).then_inc(since_exp, 1)
                split(4)
                decays(1)
                act.wait_ge(tail_diff, a + 1)
                act.activation(tail[:], tail[:], ACT.Exp, scale=1.0 / TAU).then_inc(tail_exp, 1)
                decays(2)
                copy_v(0)
                split(5)
                decays(3)
                copy_v(1)
                decays(4)
                split(6)
                exp_r(0)
                act.wait_ge(tail_turned, a + 1)
                act.activation(flat(tailT[:]), bank[1][:, 0:(TB - 1) * P], ACT.Copy).then_inc(tailT_made, 1)
                decays(5)
                decays(6)
                decays(7)
                exp_r(1)
                for c in range(TB):
                    if c % 2 == 0:
                        act.wait_ge(go_done, a * 2 + (c // 2 + 1))
                    act.activation(o_all[:, c, ds(a * DV, DV)], bank[4 + c // 2][:, (c % 2) * DV:(c % 2 + 1) * DV],
                                   ACT.Square, accum_out=oss[:, c:c + 1]).then_inc(go_squared, 1)
            for k in range(KT):
                act.wait_ge(go_turned, k + 1)
                act.activation(hT_hi[:, k, :], bank[(k + 4) % 8][:], ACT.Copy).then_inc(goT_hi_made, 1)
            out_slots(GLA_OUT_U)
            norm(3, MLP1_ADDS)
            act.dma_start(fgain[:], norm_final_g.partition_broadcast(P)).then_inc(fgain_loaded, 16)
            act.wait_ge(fgain_loaded, 16)
            act.activation(fgain[:], fgain[:], ACT.Copy, scale=ROOT_D).then_inc(fgain_scaled, 1)
            mlp(1, MLP1_U)
            norm(4, ADDS)

        @block.tensor
        def _(pe):
            def tile(out, w, x, before=None, begins=False):
                for k in range(KT):
                    if before:
                        before(k)
                    a = pe.matmul(out, w[0][:, k, :], x[1][:, k, :], start=(k == 0), stop=False)
                    if begins and k == 0:
                        a.then_inc(w_begun, 1)
                    pe.matmul(out, w[0][:, k, :], x[0][:, k, :], start=False, stop=False)
                    a = pe.matmul(out, w[1][:, k, :], x[0][:, k, :], start=False, stop=(k == KT - 1))
                return a

            def block_of_tokens(out, t, w, x, ks, first, last, begins=False):
                for m, k in enumerate(ks):
                    xs = [b[:, k, t * P:(t + 1) * P] for b in x]
                    a = pe.matmul(out, xs[0], w[1][:, m, :], start=(first and m == 0), stop=False)
                    if begins and m == 0:
                        a.then_inc(w_begun, 1)
                    pe.matmul(out, xs[0], w[0][:, m, :], start=False, stop=False)
                    a = pe.matmul(out, xs[1], w[0][:, m, :], start=False, stop=(last and m == len(ks) - 1))
                return a

            hT = (hT_hi, hT_lo)

            def unit(i, per, c, shape=None, first=0):
                return [(cols(w, c % SLOTS, shape, first) if shape else
                         w[:, c % SLOTS, :].rearrange("p (k n) -> p k n", k=KT // 2)) for w in (w_hi, w_lo)]

            def split_of(i, per, c):
                pe.wait_ge(w_lo_made, i * per + (c + 1))

            def turn_norm(n, adds=0):
                for t in range(TB):
                    pe.wait_ge(hn_made, n * TB + t + 1)
                    for k in (4, 5, 6, 7, 0, 1, 2, 3) if t < TB - 1 else range(KT):
                        if not n and t == 0 and k == 7:
                            pe.wait_ge(gain_made, 1)
                        if n and t == 0 and k < TB:
                            pe.wait_ge(added, adds - TB + k + 1)
                        a = pe.transpose(bank[k][:, t * P:(t + 1) * P], hn[:, t, k * P:(k + 1) * P], ident[:])
                        if t == TB - 1:
                            a.then_inc(hn_turned, 1)

            def ready(n):
                return lambda k: pe.wait_ge(hT_lo_made, n * KT + k + 1)

            def add_rows(i, per, c, x, ready_rows, early=False):
                for half in range(2):
                    for kg in range(2):
                        j = 2 * half + kg
                        split_of(i, per, c + j)
                        if half == 0:
                            ready_rows(kg)
                        for t in range(TB):
                            w, ks = unit(i, per, c + j), range(4 * kg, 4 * kg + 4)
                            if early and half == 0 and t == 0:
                                if kg == 0:
                                    continue
                                w, ks = [b[:, KT // 2 - 1:] for b in w], range(KT - 1, KT)
                            a = block_of_tokens(bank[sum_bank(half, t, early)][:], t, w, x, ks,
                                                kg == 0, kg == 1, t == 0)
                            if kg == 1:
                                a.then_inc(sum_done, 1)

            def mlp(layer, c, adds):
                tiles = layer * 8 * GROUPS

                def group(g):
                    for j in range(4):
                        split_of(g, 8, c + j)
                        for m in range(2):
                            t = 2 * j + m
                            if t < 4:
                                pe.wait_ge(added, g * 8 + (adds - 4 + t + 1))
                            else:
                                pe.wait_ge(u_lo_made, g * 8 + (tiles + t - 3))
                            w = [x[:, :, m * P:(m + 1) * P] for x in unit(g, 8, c + j, 256)]
                            tile(bank[t % 4][:], w, hT, ready(2 * layer + 1) if t == 0 else None,
                                 m == 0).then_inc(up_done, 1)
                    add_rows(g, 8, c + 4, (u_hi, u_lo),
                             lambda kg: pe.wait_ge(u_lo_made, g * 8 + (tiles + 4 * kg + 4)))

                with pe.Fori(0, GROUPS - 1) as g:
                    group(g)
                group(GROUPS - 1)

            pe.wait_ge(ident_made, 1)
            pe.wait_ge(gain_loaded, 32)
            pe.transpose(bank[7][:, 0:4 * KT], gain_rows[:], ident[0:4 * KT, 0:4 * KT]).then_inc(gain_turned, 1)
            turn_norm(0)

            def project_q(n, b):
                i = n * 2 + (b + 1)
                c = FOX_U + 2 * b + 2
                split_of(n, 4, c)
                if b >= 0:
                    pe.wait_ge(v_copied, i)
                tile(bank[0][:], unit(n, 4, c, P), hT, ready(0) if b < 0 else None, True).then_inc(q_done, 1)

            def project_k(n, b):
                i = n * 2 + (b + 1)
                pe.wait_ge(q_copied, i * 2 + 2)
                tile(bank[0][:], unit(n, 4, FOX_U + 2 * b + 2, P, UNIT // 2), hT).then_inc(k_done, 1)

            def project_v(n, b):
                i = n * 2 + (b + 1)
                split_of(n, 4, FOX_U + 2 * b + 3)
                pe.wait_ge(k_copied, i + 1)
                tile(bank[0][:], unit(n, 4, FOX_U + 2 * b + 3, P), hT, None, True).then_inc(vT_done, 1)

            def turn_v(n, b):
                i = n * 2 + (b + 1)
                pe.wait_ge(vT_copied, i + 1)
                for t in range(TB):
                    a = pe.transpose(bank[0][:, t * P:(t + 1) * P], vT[:, t * P:(t + 1) * P], ident[:])
                a.then_inc(v_turned, 1)

            def scores(i, b, a):
                head = i * 2 + a
                if a == 0:
                    pe.wait_ge(q_copied, i * 2 + 2)
                    pe.wait_ge(k_copied, i + 1)
                for m, (t, bk, first) in enumerate(SCORES):
                    w = (t + 1) * P
                    to = bank[bk][:, first:first + w]
                    pe.matmul(to, qz[:, b, a, t * P:(t + 1) * P], kT[:, 0:w], start=True, stop=False)
                    pe.matmul(to, sel[:, ds(head, 1)].to_broadcast([96, P]), c3[:, 0:w],
                              start=False, stop=False)
                    mm = pe.matmul(bank[bk][:, first + w - P:first + w], ident16[:], causal16[:],
                                   start=False, stop=True)
                    if m != 2:
                        mm.then_inc(scores_done, 1)

            def turn_probs(head):
                pe.wait_ge(probs_made, head * 4 + 4)
                for bk, places in TURNED:
                    for t, j, at in places:
                        a = pe.transpose(bank[bk][:, at:at + P], probs[:, OFF[t] + j * P:OFF[t] + (j + 1) * P], ident[:])
                    a.then_inc(probs_turned, 1)

            def values(i, a):
                head = i * 2 + a
                if a == 0:
                    pe.wait_ge(v_copied, i + 1)
                pe.wait_ge(pT_act, head * 2 + 2)
                pe.wait_ge(pT_dve, head + 1)
                if not (isinstance(head, int) and head == 0):
                    pe.wait_ge(o_lo_made, head + o_before)
                for j, at in enumerate((0, 512, 1024, 896)):
                    mm = pe.matmul(bank[1][:, j * P:], v[:, j, :], probsT[:, at:at + S - j * P],
                                   start=(j == 0), stop=(j == TB - 1))
                mm.then_inc(o_done, 1)

            def out_early(kg):
                split_of(0, 0, FOX_OUT_U + kg)
                if kg == 0:
                    pe.wait_ge(v_copied, PAIRS)
                pe.wait_ge(o_lo_made, 2 * (4 + 3 * kg) + o_before)
                block_of_tokens(bank[0][:], 0, unit(0, 0, FOX_OUT_U + kg), (oT_hi, oT_lo),
                                (range(4), range(4, KT - 1))[kg], kg == 0, False, kg == 0)

            def fox_pair(n, b, following=True):
                i = n * 2 + b
                scores(i, b, 0)
                if following:
                    project_q(n, b)
                else:
                    out_early(0)
                turn_probs(i * 2)
                scores(i, b, 1)
                values(i, 0)
                if following:
                    project_k(n, b)
                else:
                    out_early(1)
                turn_probs(i * 2 + 1)
                if following:
                    project_v(n, b)
                values(i, 1)
                if following:
                    turn_v(n, b)

            o_before = 1
            project_q(0, -1)
            tile(bank[1][0:FOX_H, :], (gate_hi[:, 0], gate_lo[:, 0]), hT,
                 lambda k: pe.wait_ge(gate_lo_made, 1) if k == 0 else None).then_inc(f_done, 1)
            project_k(0, -1)
            project_v(0, -1)
            turn_v(0, -1)
            pe.wait_ge(fox_consts_made, 3)
            pe.wait_ge(c3_made, 3)
            with pe.Fori(0, PAIRS // 2 - 1) as n:
                fox_pair(n, 0)
                fox_pair(n, 1)
            fox_pair(PAIRS // 2 - 1, 0)
            fox_pair(PAIRS // 2 - 1, 1, False)
            add_rows(0, 0, FOX_OUT_U, (oT_hi, oT_lo), lambda kg: pe.wait_ge(o_lo_made, 8 * kg + 8 + 1), True)
            turn_norm(1, MLP0_ADDS)
            mlp(0, MLP0_U, MLP0_ADDS)
            turn_norm(2, GLA_ADDS)

            tile(bank[0][0:RANK, :], (gate_hi[:, 1], gate_lo[:, 1]), hT, ready(2)).then_inc(z_done, 1)
            pe.wait_ge(gup_loaded, 32)
            pe.wait_ge(z_copied, 1)
            for a in range(GLA_H):
                pe.matmul(bank[3 + a][:], gup[:, a * DK:(a + 1) * DK], zT[0:RANK + 1, :],
                          start=True, stop=True).then_inc(gate_done, 1)
            with pe.Fori(0, GLA_H) as a:
                def tokens(j, t, banks, begins, done):
                    mm = block_of_tokens(bank[banks + t // 2][:, (t % 2) * DV:(t % 2 + 1) * DV], t,
                                         unit(a, 4, GLA_U + j, DV), hT, range(KT), True, True, begins)
                    if t % 2:
                        mm.then_inc(done, 1)

                def level(lv):
                    if lv:
                        pe.wait_ge(ql_made, a * (2 * LEVELS) + 2 * lv)
                        qs, ks = ql[:, lv % 2, :], kl[:, lv % 2, :]
                    else:
                        pe.wait_ge(gk_copied, a + 1)
                        pe.wait_ge(gq_copied, a + 1)
                        qs, ks = gq, gk
                    if lv >= 2:
                        pe.wait_ge(level_kept, a * (LEVELS + 1) + (lv - 1))
                    for t in range(TB):
                        mm = pe.matmul(bank[LEVEL_BANK[lv % 2]][:, t * P:(t + 1) * P], ks[:, t * P:(t + 1) * P],
                                       qs[:, t * P:(t + 1) * P], start=True, stop=True)
                    mm.then_inc(level_done, 1)

                split_of(a, 4, GLA_U)
                tile(bank[0][:], unit(a, 4, GLA_U, DK), hT, None, True).then_inc(gq_done, 1)
                split_of(a, 4, GLA_U + 1)
                tile(bank[1][:], unit(a, 4, GLA_U + 1, DK), hT, None, True).then_inc(gk_done, 1)
                split_of(a, 4, GLA_U + 2)
                pe.wait_ge(g_min, GLA_H)
                tokens(2, 0, 3, True, gv_done)
                tokens(2, 1, 3, False, gv_done)
                level(0)
                pe.wait_ge(go_made, a * TB + GO_BASE)
                tokens(2, 2, 3, False, gv_done)
                level(1)
                tokens(2, 3, 3, False, gv_done)
                level(2)
                split_of(a, 4, GLA_U + 3)
                tokens(3, 0, 5, True, r_done)
                level(3)
                tokens(3, 1, 5, False, r_done)
                pe.wait_ge(ktail_made, a + 1)
                for c in range(TB - 1):
                    mm = pe.transpose(bank[1][:, c * P:(c + 1) * P], tail[:, c, :], ident[:])
                mm.then_inc(tail_turned, 1)
                level(4)
                tokens(3, 2, 5, False, r_done)
                level(5)
                pe.wait_ge(tailT_made, a + 1)
                pe.wait_ge(gv_copied, a * 2 + 2)
                for c in range(TB - 1):
                    mm = pe.matmul(bank[2 + c // 2][:, (c % 2) * DV:(c % 2 + 1) * DV], tailT[:, c, :], gv[:, c, :],
                                   start=True, stop=True)
                mm.then_inc(kv_done, 1)
                level(6)
                tokens(3, 3, 5, False, r_done)
                level(7)
                pe.wait_ge(silu_made, a * 2 + 1)
                pe.wait_ge(qsince_made, a + 1)
                to = [bank[4 + c // 2][:, (c % 2) * DV:(c % 2 + 1) * DV] for c in range(TB)]
                for c in range(1, TB):
                    pe.wait_ge(state_made, a * (TB - 1) + c)
                    pe.matmul(to[c], since[:, c, :], state[:, c - 1, :], start=(c < 3), stop=False,
                              skip_group_check=True)
                pe.wait_ge(level_kept, a * (LEVELS + 1) + LEVELS + 1)
                for c in range(TB):
                    mm = pe.matmul(to[c], attnT[:, c, :], gv[:, c, :], start=False, stop=True,
                                   skip_group_check=True)
                    if c % 2:
                        mm.then_inc(go_done, 1)
            pe.wait_ge(go_made, GLA_H * TB + GO_BASE)
            for k in range(KT):
                for t in range(TB):
                    mm = pe.transpose(bank[(k + 4) % 8][:, t * P:(t + 1) * P], o_all[:, t, k * P:(k + 1) * P], ident[:])
                mm.then_inc(go_turned, 1)
            add_rows(0, 0, GLA_OUT_U, hT, lambda kg: pe.wait_ge(goT_lo_made, 4 * kg + 4))
            turn_norm(3, MLP1_ADDS)
            mlp(1, MLP1_U, MLP1_ADDS)

        @block.vector
        def _(dve):
            mine = Steps(dve, dve_step)

            def split_lo(i, per, c, n=UNIT):
                slot = c % SLOTS
                dve.wait_ge(w_hi_made, i * per + (c + 1))
                dve.tensor_tensor(w_lo[:, slot, 0:n], w_stage[:, slot, 0:n], fp(w_hi[:, slot, 0:n]),
                                  ALU.subtract).then_inc(w_lo_made, 1)

            def norm_block(n, t):
                dve.wait_ge(rstd_made, n * TB + t + 1)
                if n < 4:
                    dve.tensor_scalar(hn[:, t, :], h[:, t, :], rstd[:, t:t + 1], ROOT_D, ALU.mult,
                                      ALU.mult).then_inc(hn_made, 1)
                else:
                    if t == 0:
                        dve.wait_ge(fgain_scaled, 1)
                    dve.scalar_tensor_tensor(out=hn[:, t, :], in0=h[:, t, :], scalar=rstd[:, t:t + 1],
                                             in1=fgain[:], op0=ALU.mult, op1=ALU.mult).then_inc(y_made, 1)

            def norm_lo(n):
                if n == 0:
                    dve.wait_ge(gain_made, 1)
                for k in range(KT):
                    dve.wait_ge(hT_hi_made, n * KT + k + 1)
                    dve.scalar_tensor_tensor(out=hT_lo[:, k, :], in0=bank[k][:], scalar=gain[:, GAIN[n], k:k + 1],
                                             in1=fp(hT_hi[:, k, :]), op0=ALU.mult,
                                             op1=ALU.subtract).then_inc(hT_lo_made, 1)

            def add(half, t, count, early=False):
                dve.wait_ge(sum_done, count)
                to = h[:, t, half * S:(half + 1) * S]
                dve.tensor_tensor(to, bank[sum_bank(half, t, early)][:], to, ALU.add).then_inc(added, 1)

            def add_slots(i, per, c, adds, n=None, splits=4, early=False):
                for j in range(4):
                    if j < splits:
                        split_lo(i, per, c + j + 3)
                    if j % 2:
                        for t in range(TB):
                            add(j // 2, t, i * 8 + (adds + 4 * (j // 2) + t + 1), early)
                            if n is not None and j == 3:
                                norm_block(n, t)

            def mlp(layer, c, adds):
                tiles = layer * 8 * GROUPS

                def group(g, last=False):
                    for j in range(4):
                        split_lo(g, 8, c + j + 3)
                        for t in (2 * j, 2 * j + 1):
                            dve.wait_ge(relu_made, g * 8 + (tiles + t + 1))
                            dve.tensor_tensor(u_sq[:, t % 4, :], relu[:, t % 4, :], relu[:, t % 4, :],
                                              ALU.mult).then_inc(u_made, 1)
                            dve.wait_ge(u_made, g * 8 + (tiles + t + 1))
                            dve.wait_ge(u_hi_made, g * 8 + (tiles + t + 1))
                            dve.tensor_tensor(u_lo[:, t, :], u_sq[:, t % 4, :], fp(u_hi[:, t, :]),
                                              ALU.subtract).then_inc(u_lo_made, 1)
                    add_slots(g, 8, c + 4, adds, 2 * layer + 2 if last else None,
                              1 if last and layer == 1 else 4)

                with dve.Fori(0, GROUPS - 1) as g:
                    group(g)
                group(GROUPS - 1, True)
                if layer == 0:
                    norm_lo(2)

            for t in range(TB):
                norm_block(0, t)
            split_lo(0, 0, 0)
            norm_lo(0)
            dve.wait_ge(gate_hi_made, 1)
            dve.tensor_tensor(gate_lo[:], gate_w[:], fp(gate_hi[:]), ALU.subtract).then_inc(gate_lo_made, 1)
            split_lo(0, 0, 1, UNIT // 2)
            split_lo(0, 0, 2)
            split_lo(0, 0, 3, UNIT // 2)
            dve.wait_ge(f_abs, 1)
            mine.then(dve.tensor_scalar(fg[:, 1, :], bank[1][0:FOX_H, :], bf_col[:, 0:1], 0.0, ALU.add, ALU.min))
            dve.wait_ge(f_ln, 1)
            mine.then(dve.tensor_tensor(fg[:, 1, :], fg[:, 1, :], fg[:, 0, :], ALU.subtract))
            mine.then(dve.memset(fg[:, 0, :], 1.0))
            mine.then(dve.tensor_tensor_scan(fg[:, 1, :], fg[:, 0, :], fg[:, 1, :], 0.0, ALU.mult, ALU.add))
            dve.wait_ge(fox_consts_made, 3)
            for j in range(3):
                if j < 2:
                    mine.then(dve.tensor_copy(fg16[:, j, :], fg[:, 1, :]))
                    dve.tensor_copy(c3[32 * j:32 * j + FOX_H, :], fg16[:, j, :]).then_inc(c3_made, 1)
                    mine.then(dve.tensor_tensor(fg[:, 1, :], fg[:, 1, :], fg16[:, j, :], ALU.subtract))
                else:
                    dve.tensor_copy(c3[32 * j:32 * j + FOX_H, :], fg[:, 1, :]).then_inc(c3_made, 1)

            def copy_vT(i):
                dve.wait_ge(vT_done, i + 1)
                dve.tensor_copy(vT[:], bank[0][:]).then_inc(vT_copied, 1)

            def copy_v(i):
                dve.wait_ge(v_turned, i + 1)
                dve.tensor_copy(flat(v[:]), bank[0][:]).then_inc(v_copied, 1)

            def maxima(head, a):
                for m, ts in enumerate(((3,), (2,), (1, 0))):
                    dve.wait_ge(scores_done, head * 3 + m + 1)
                    for t, b, first in SCORES:
                        if t in ts:
                            mine.then(dve.tensor_reduce(mx[:, t:t + 1], bank[b][:, first:first + (t + 1) * P],
                                                        AX_X, ALU.max))
                    lo = min(ts)
                    dve.tensor_scalar(nmx[:, a, lo:lo + len(ts)], mx[:, lo:lo + len(ts)], -1.0, None,
                                      ALU.mult).then_inc(nmx_made, 1)

            def normalise(head):
                dve.wait_ge(exp_made, head * 4 + 4)
                mine.then(dve.reciprocal(rinv[:], rsum[:]))
                for t in range(TB):
                    part = probs[:, OFF[t]:OFF[t] + (t + 1) * P]
                    dve.tensor_scalar(part, part, rinv[:, t:t + 1], None, ALU.mult).then_inc(probs_made, 1)

            def copy_pT(head):
                dve.wait_ge(probs_turned, head * 3 + 2)
                dve.tensor_copy(probsT[:, 512:1024], bank[6][:]).then_inc(pT_dve, 1)

            def keep_o(i, a):
                rows = slice(a * FOX_HD, (a + 1) * FOX_HD)
                dve.wait_ge(o_hi_made, i * 2 + (a + 1))
                at = oT_lo[rows, ds(i, 1), :].rearrange("p a n -> p (a n)")
                hi = fp(oT_hi[rows, ds(i, 1), :]).rearrange("p a n -> p (a n)")
                dve.tensor_tensor(at, bank[1][rows, :], hi, ALU.subtract).then_inc(o_lo_made, 1)

            def fox_pair(n, b, following=True):
                i = n * 2 + b
                maxima(i * 2, 0)
                if following:
                    split_lo(n, 4, 2 * b + 5, UNIT // 2 if not isinstance(n, int) else UNIT)
                normalise(i * 2)
                copy_pT(i * 2)
                maxima(i * 2 + 1, 1)
                keep_o(i, 0)
                normalise(i * 2 + 1)
                copy_pT(i * 2 + 1)
                if following:
                    split_lo(n, 4, 2 * b + 6)
                    copy_vT(i + 1)
                keep_o(i, 1)
                if following:
                    copy_v(i + 1)

            dve.wait_ge(c3_made, 3)
            dve.memset(fg[0:1, 0, 0:1], 0.0).then_inc(o_lo_made, 1)
            split_lo(0, 0, 4)
            copy_vT(0)
            copy_v(0)
            with dve.Fori(0, PAIRS // 2 - 1) as n:
                mine.enter(n, 20)
                fox_pair(n, 0)
                fox_pair(n, 1)
            mine.leave(PAIRS // 2 - 1)
            fox_pair(PAIRS // 2 - 1, 0)
            fox_pair(PAIRS // 2 - 1, 1, False)
            add_slots(0, 0, FOX_OUT_U, FOX_ADDS, 1, early=True)
            norm_lo(1)
            mlp(0, MLP0_U, MLP0_ADDS)

            dve.wait_ge(gla_filled, 5)
            dve.tensor_tensor(xor[:], xor[:], other[:], ALU.bitwise_xor).then_inc(xor_made, 1)
            for a in range(GLA_H):
                dve.wait_ge(g_abs, a + 1)
                dve.tensor_scalar(gb[:, a, :], bank[3 + a][:], 0.0, None, ALU.min).then_inc(g_min, 1)
            dve.wait_ge(xor_cut, 1)
            for lv in range(1, LEVELS + 1):
                half = P >> lv
                mine.then(dve.tensor_scalar(ge[:], xor[:], float(half), None, ALU.is_ge))
                dve.scalar_tensor_tensor(out=masks[:, lv - 1, :], in0=xor[:], scalar=float(2 * half), in1=ge[:],
                                         op0=ALU.is_lt, op1=ALU.mult).then_inc(masks_made, 1)
                dve.wait_ge(masks_made, lv)
            dve.wait_ge(g_ln, 1)
            dve.wait_ge(g_min, GLA_H)
            mine.then(dve.tensor_tensor(gb[:], gb[:], glog[:], ALU.subtract))
            for a in range(GLA_H):
                dve.tensor_tensor_scan(gb[:, a, :], flat(restart[:]), gb[:, a, :], 0.0, ALU.mult,
                                       ALU.add).then_inc(gb_made, 1)
            dve.wait_ge(gb_made, GLA_H)
            dve.wait_ge(levels_zeroed, 2)
            dve.wait_ge(gn_scaled, 1)
            dve.memset(through[:], 0.0).then_inc(go_made, 1)

            with dve.Fori(0, GLA_H) as a:
                mine.enter(a, 6)
                b = gb[:, ds(a, 1), :].rearrange("p a n -> p (a n)")

                def split(j):
                    split_lo(a, 4, GLA_U + j)

                def differences(lv):
                    half = P >> lv
                    if lv > 2:
                        dve.wait_ge(ql_made, a * (2 * LEVELS) + 2 * (lv - 2))
                    left, right = halves(b, half)
                    to_left, to_right = halves(decay[:, lv % 2, :], half)
                    middle = left[:, :, half - 1:half].to_broadcast([P, S // (2 * half), half])
                    dve.tensor_tensor(to_left, middle, left, ALU.subtract).then_inc(half_diff, 1)
                    dve.tensor_tensor(to_right, right, middle, ALU.subtract).then_inc(diff_made, 1)

                def decayed(lv):
                    half = P >> lv
                    dve.wait_ge(decay_made, a * LEVELS + lv)
                    dl, dr = halves(decay[:, lv % 2, :], half)
                    dve.tensor_tensor(halves(ql[:, lv % 2, :], half)[1], halves(gq[:], half)[1], dr,
                                      ALU.mult).then_inc(ql_made, 1)
                    dve.tensor_tensor(halves(kl[:, lv % 2, :], half)[0], halves(gk[:], half)[0], dl,
                                      ALU.mult).then_inc(ql_made, 1)

                def keep(lv):
                    dve.wait_ge(level_done, a * (LEVELS + 1) + (lv + 1))
                    got = bank[LEVEL_BANK[lv % 2]][:].rearrange("p (c n) -> p c n", c=TB)
                    if lv == 0:
                        dve.tensor_tensor(attnT[:], got, ident[:].unsqueeze(1).to_broadcast([P, TB, P]),
                                          ALU.mult).then_inc(level_kept, 1)
                    else:
                        dve.wait_ge(level_kept, a * (LEVELS + 1) + lv)
                        dve.memset(turn[:], 0.0)
                        dve.copy_predicated(attnT[:], masks[:, lv - 1, :].unsqueeze(1).to_broadcast([P, TB, P]),
                                            got).then_inc(level_kept, 1)

                def gates(j):
                    dve.wait_ge(er_made, a * 2 + (j + 1))
                    to = silu[:, 2 * j:2 * j + 2, :]
                    mine.then(dve.tensor_scalar(to, to, 1.0, None, ALU.add))
                    mine.then(dve.reciprocal(to, to))
                    mine.then(dve.tensor_tensor(flat(to), bank[5 + j][:], flat(to), ALU.mult))
                    dve.tensor_tensor(to, to, gn[:].unsqueeze(1).to_broadcast([P, 2, DV]),
                                      ALU.mult).then_inc(silu_made, 1)

                split(3)
                differences(1)
                split(4)
                dve.wait_ge(gk_done, a + 1)
                dve.tensor_copy(gk[:], bank[1][:]).then_inc(gk_copied, 1)
                b3 = b.rearrange("p (c n) -> p c n", c=TB)[:, 0:TB - 1, :]
                dve.tensor_tensor(tail[:], b3[:, :, P - 1:P].to_broadcast([P, TB - 1, P]), b3,
                                  ALU.subtract).then_inc(tail_diff, 1)
                differences(2)
                dve.wait_ge(gq_copied, a + 1)
                dve.wait_ge(gk_copied, a + 1)
                decayed(1)
                keep(0)
                dve.wait_ge(since_exp, a + 1)
                dve.tensor_copy(through[:].unsqueeze(2), since[:, :, P - 1:P]).then_inc(through_made, 1)
                differences(3)
                decayed(2)
                split(5)
                keep(1)
                differences(4)
                decayed(3)
                keep(2)
                differences(5)
                decayed(4)
                keep(3)
                split(6)
                differences(6)
                decayed(5)
                keep(4)
                differences(7)
                decayed(6)
                gates(0)
                keep(5)
                decayed(7)
                dve.wait_ge(kv_done, a + 1)
                dve.tensor_copy(state[:, 0, :], bank[2][:, 0:DV]).then_inc(state_made, 1)
                for c in range(1, TB - 1):
                    dve.wait_ge(through_made, a + 1)
                    dve.wait_ge(state_made, a * (TB - 1) + c)
                    dve.scalar_tensor_tensor(out=state[:, c, :], in0=state[:, c - 1, :], scalar=through[:, c:c + 1],
                                             in1=bank[2 + c // 2][:, (c % 2) * DV:(c % 2 + 1) * DV],
                                             op0=ALU.mult, op1=ALU.add).then_inc(state_made, 1)
                keep(6)
                keep(7)
                gates(1)
                dve.wait_ge(silu_made, a * 2 + 2)
                for j in range(2):
                    dve.wait_ge(orstd_made, a * 2 + (j + 1))
                    for c in (2 * j, 2 * j + 1):
                        dve.scalar_tensor_tensor(out=o_all[:, c, ds(a * DV, DV)],
                                                 in0=bank[4 + j][:, (c % 2) * DV:(c % 2 + 1) * DV],
                                                 scalar=orstd[:, c:c + 1], in1=silu[:, c, :],
                                                 op0=ALU.mult, op1=ALU.mult).then_inc(go_made, 1)
            mine.leave(GLA_H)
            for k in range(KT):
                dve.wait_ge(goT_hi_made, k + 1)
                dve.tensor_tensor(hT_lo[:, k, :], bank[(k + 4) % 8][:], fp(hT_hi[:, k, :]), ALU.subtract).then_inc(goT_lo_made, 1)
            add_slots(0, 0, GLA_OUT_U, GLA_ADDS, 3)
            norm_lo(3)
            mlp(1, MLP1_U, MLP1_ADDS)


_INS = ['x', 'fox_w_in', 'fox_b_f', 'fox_w_out', 'gla_w_in', 'gla_w_gate_up', 'gla_b_gate', 'gla_norm_g',
        'gla_w_out', 'mlp_w_up', 'mlp_w_down', 'norm_mix_g', 'norm_mlp_g', 'norm_final_g']
_OUTS = [((1, S, D), 'float32')]


def kernel(**inputs):
    import numpy as _np
    import concourse.bacc as _bacc
    from concourse import mybir as _mybir
    from concourse.bass_utils import run_bass_kernel_spmd as _run

    nc = _bacc.Bacc("TRN2", target_bir_lowering=False, num_devices=1)
    arrays, args = {}, []
    for name in _INS:
        a = _np.ascontiguousarray(inputs[name])
        arrays[f"in_{name}_dram"] = a
        args.append(nc.dram_tensor(f"in_{name}_dram", a.shape, _mybir.dt.from_np(a.dtype), kind="ExternalInput").ap())
    for i, (shape, dtype) in enumerate(_OUTS):
        dt = _mybir.dt.from_np(_np.dtype(dtype))
        args.append(nc.dram_tensor(f"out_{i}_dram", shape, dt, kind="ExternalOutput").ap())
    fox_gla_trunk(nc, *args)
    r = _run(nc, [arrays], core_ids=[0])
    got = tuple(r.results[0][f"out_{i}_dram"] for i in range(len(_OUTS)))
    return got[0]
```
